# Optimizing a Trainium2 kernel written in Bass

```python
import math
import jax, jax.numpy as jnp
from jax import lax
import numpy as np

D_MODEL = 1024
BATCH = 1
SEQ = 1024
DEPTH = 2

CTX_LEN = 256
GRID_W = 64
N_MIXERS = 2
N_HEADS = 16
N_KV_HEADS = 4
HEAD_DIM = D_MODEL // N_HEADS
GROUP = N_HEADS // N_KV_HEADS
Q_WIDTH = N_HEADS * HEAD_DIM
KV_WIDTH = N_KV_HEADS * HEAD_DIM
WINDOW = 128
Q_BLOCK = 128
ROPE_BASE = 10000.0
AXIS_ROT = HEAD_DIM // 2
F_GROUPS = 4
N_EXPERTS = 64
TOP_K = 8
N_EXPERT_GROUPS = 8
TOPK_GROUPS = 4
EXPERT_FF = D_MODEL // 4
SHARED_FF = D_MODEL // 4
ROUTED_SCALE = 2.5
MOE_BLOCK = 128
N_ATTN_LAYERS = (DEPTH + N_MIXERS - 1) // N_MIXERS
N_FNET_LAYERS = DEPTH // N_MIXERS
DEEPNORM_ALPHA = (2.0 * DEPTH) ** 0.25
DEEPNORM_BETA = (8.0 * DEPTH) ** -0.25
LN_EPS = 1e-5
MOD_EPS = 1e-6

kernel_name = "hybrid_swa_fnet_moe_diffusion_trunk"

def _normalize(x, eps):
    xf = x.astype(jnp.float32)
    mu = jnp.mean(xf, axis=-1, keepdims=True)
    var = jnp.mean(jnp.square(xf - mu), axis=-1, keepdims=True)
    return (xf - mu) * lax.rsqrt(var + eps)

def modulate(x, shift, scale):
    return (_normalize(x, MOD_EPS) * (1.0 + scale.astype(jnp.float32)) + shift.astype(jnp.float32)).astype(x.dtype)

def post_norm(x, y, g, b):
    z = DEEPNORM_ALPHA * x.astype(jnp.float32) + y.astype(jnp.float32)
    return (_normalize(z, LN_EPS) * g.astype(jnp.float32) + b.astype(jnp.float32)).astype(x.dtype)

def axial_rope_tables(L):
    rows = L // GRID_W
    r = jnp.repeat(jnp.arange(rows, dtype=jnp.float32), GRID_W)
    col = jnp.tile(jnp.arange(GRID_W, dtype=jnp.float32), rows)
    inv = ROPE_BASE ** (-jnp.arange(0, AXIS_ROT, 2, dtype=jnp.float32) / AXIS_ROT)
    ar = r[:, None] * inv
    ac = col[:, None] * inv
    ang = jnp.concatenate([ar, ar, ac, ac], axis=-1)
    return jnp.cos(ang), jnp.sin(ang)

def _rot_half(t):
    a, b = jnp.split(t, 2, axis=-1)
    return jnp.concatenate([-b, a], axis=-1)

def apply_rope(x, cos, sin):
    xr, xc = jnp.split(x, 2, axis=-1)
    rot = jnp.concatenate([_rot_half(xr), _rot_half(xc)], axis=-1)
    c = cos[None, :, None, :]
    s = sin[None, :, None, :]
    return (x.astype(jnp.float32) * c + rot.astype(jnp.float32) * s).astype(x.dtype)

def sink_attend(qb, keys, values, masks, sinks):
    B, Q = qb.shape[0], qb.shape[1]
    scale = HEAD_DIM ** -0.5
    parts = []
    for kk, m in zip(keys, masks):
        s = jnp.einsum('bqhgd,bkhd->bhgqk', qb, kk).astype(jnp.float32) * scale
        if m is not None:
            s = jnp.where(m, s, -jnp.inf)
        parts.append(s)
    sink = jnp.broadcast_to(sinks.astype(jnp.float32).reshape(1, N_KV_HEADS, GROUP, 1, 1),
                            (B, N_KV_HEADS, GROUP, Q, 1))
    p = jax.nn.softmax(jnp.concatenate(parts + [sink], axis=-1), axis=-1).astype(qb.dtype)
    out = None
    start = 0
    for vv in values:
        n = vv.shape[1]
        o = jnp.einsum('bhgqk,bkhd->bqhgd', p[..., start:start + n], vv)
        out = o if out is None else out + o
        start += n
    return out

def windowed_attention(q, k, v, k_ctx, v_ctx, sinks):
    B, L = q.shape[0], q.shape[1]
    nb = L // Q_BLOCK
    span = Q_BLOCK + 2 * WINDOW
    pad = ((0, 0), (WINDOW, WINDOW), (0, 0), (0, 0))
    k_pad = jnp.pad(k, pad)
    v_pad = jnp.pad(v, pad)
    offs = jnp.arange(span) - WINDOW
    qi = jnp.arange(Q_BLOCK)

    def one_block(b):
        q0 = b * Q_BLOCK
        qb = lax.dynamic_slice_in_dim(q, q0, Q_BLOCK, axis=1)
        kb = lax.dynamic_slice_in_dim(k_pad, q0, span, axis=1)
        vb = lax.dynamic_slice_in_dim(v_pad, q0, span, axis=1)
        kpos = q0 + offs
        mask = (jnp.abs(qi[:, None] - offs[None, :]) <= WINDOW) & ((kpos >= 0) & (kpos < L))[None, :]
        return sink_attend(qb, (kb, k_ctx), (vb, v_ctx), (mask, None), sinks)

    o = lax.map(one_block, jnp.arange(nb))
    return jnp.moveaxis(o, 0, 1).reshape(B, L, N_KV_HEADS, GROUP, HEAD_DIM)

def attention_mixer(u, u_ctx, w_qkv, w_o, sinks, cos, sin, ctx_out):
    B, L, _ = u.shape
    C = u_ctx.shape[1]
    qkv = u @ w_qkv
    q = apply_rope(qkv[..., :Q_WIDTH].reshape(B, L, N_HEADS, HEAD_DIM), cos, sin)
    k = apply_rope(qkv[..., Q_WIDTH:Q_WIDTH + KV_WIDTH].reshape(B, L, N_KV_HEADS, HEAD_DIM), cos, sin)
    v = qkv[..., Q_WIDTH + KV_WIDTH:].reshape(B, L, N_KV_HEADS, HEAD_DIM)
    q = q.reshape(B, L, N_KV_HEADS, GROUP, HEAD_DIM)
    if ctx_out:
        qkv_c = u_ctx @ w_qkv
        q_c = qkv_c[..., :Q_WIDTH].reshape(B, C, N_KV_HEADS, GROUP, HEAD_DIM)
        kv_c = qkv_c[..., Q_WIDTH:]
    else:
        kv_c = u_ctx @ w_qkv[:, Q_WIDTH:]
    k_c = kv_c[..., :KV_WIDTH].reshape(B, C, N_KV_HEADS, HEAD_DIM)
    v_c = kv_c[..., KV_WIDTH:].reshape(B, C, N_KV_HEADS, HEAD_DIM)
    o = windowed_attention(q, k, v, k_c, v_c, sinks)
    y = o.reshape(B, L, Q_WIDTH) @ w_o
    if not ctx_out:
        return y, None
    o_c = sink_attend(q_c, (k_c,), (v_c,), (None,), sinks)
    return y, o_c.reshape(B, C, Q_WIDTH) @ w_o

def fourier_mixer(u, w_f):
    B, L, D = u.shape
    ug = u.reshape(B, L, F_GROUPS, D // F_GROUPS).astype(jnp.float32)
    f = jnp.fft.fft2(ug, axes=(1, 3), norm='ortho').real
    return f.reshape(B, L, D).astype(u.dtype) @ w_f

def moe_ffn(tok, router_w, router_bias, w_gate, w_up, w_down, s_gate, s_up, s_down):
    T, D = tok.shape
    per_group = N_EXPERTS // N_EXPERT_GROUPS
    scores = jax.nn.sigmoid((tok @ router_w).astype(jnp.float32))
    sel = scores + router_bias.astype(jnp.float32)
    group_score = lax.top_k(sel.reshape(T, N_EXPERT_GROUPS, per_group), 2)[0].sum(-1)
    _, top_groups = lax.top_k(group_score, TOPK_GROUPS)
    group_ok = (top_groups[:, :, None] == jnp.arange(N_EXPERT_GROUPS)[None, None, :]).any(axis=1)
    sel = jnp.where(jnp.repeat(group_ok, per_group, axis=1), sel, -jnp.inf)
    _, top_e = lax.top_k(sel, TOP_K)
    wts = jnp.take_along_axis(scores, top_e, axis=-1)
    wts = wts / jnp.sum(wts, axis=-1, keepdims=True) * ROUTED_SCALE

    TK = T * TOP_K
    flat_e = top_e.reshape(-1)
    flat_tok = jnp.arange(TK, dtype=jnp.int32) // TOP_K
    flat_w = wts.reshape(-1)
    order = jnp.argsort(flat_e)
    e_s, tok_s, w_s = flat_e[order], flat_tok[order], flat_w[order]
    counts = jnp.bincount(flat_e, length=N_EXPERTS)
    starts = jnp.cumsum(counts) - counts
    padded = (counts + MOE_BLOCK - 1) // MOE_BLOCK * MOE_BLOCK
    pend = jnp.cumsum(padded)
    pstarts = pend - padded
    dest = pstarts[e_s] + jnp.arange(TK) - starts[e_s]
    n_blocks = -(-TK // MOE_BLOCK) + N_EXPERTS
    cap = n_blocks * MOE_BLOCK
    tok_buf = jnp.full((cap,), T, jnp.int32).at[dest].set(tok_s.astype(jnp.int32))
    w_buf = jnp.zeros((cap,), tok.dtype).at[dest].set(w_s.astype(tok.dtype))
    block_e = jnp.clip(jnp.searchsorted(pend, jnp.arange(n_blocks) * MOE_BLOCK, side='right'), 0, N_EXPERTS - 1)
    x_pad = jnp.concatenate([tok, jnp.zeros((1, D), tok.dtype)], axis=0)

    def body(y, b):
        rows = lax.dynamic_slice_in_dim(tok_buf, b * MOE_BLOCK, MOE_BLOCK)
        wb = lax.dynamic_slice_in_dim(w_buf, b * MOE_BLOCK, MOE_BLOCK)
        e = block_e[b]
        xb = x_pad[rows]
        hb = jax.nn.silu(xb @ w_gate[e]) * (xb @ w_up[e])
        return y.at[rows].add((hb @ w_down[e]) * wb[:, None]), None

    y, _ = lax.scan(body, jnp.zeros_like(x_pad), jnp.arange(n_blocks))
    shared = (jax.nn.silu(tok @ s_gate) * (tok @ s_up)) @ s_down
    return y[:T] + shared

def setup_inputs(seed: int = 0) -> dict:
    key = jax.random.key(seed)
    ks = jax.random.split(key, 20)
    f32 = jnp.float32
    D = D_MODEL

    def nrm(k, shape, s):
        return jax.random.normal(k, shape, f32) * s

    qkv_col_scale = jnp.concatenate([jnp.ones((Q_WIDTH + KV_WIDTH,), f32),
                                     jnp.full((KV_WIDTH,), DEEPNORM_BETA, f32)])
    return {
        "x": nrm(ks[0], (BATCH, SEQ, D), 1.0),
        "c": nrm(ks[1], (BATCH, D), 1.0),
        "ctx": nrm(ks[2], (BATCH, CTX_LEN, D), 1.0),
        "c_ctx": nrm(ks[3], (D,), 1.0),
        "w_ada": nrm(ks[4], (DEPTH, D, 6 * D), D ** -0.5),
        "b_ada": nrm(ks[5], (DEPTH, 6 * D), 0.02),
        "ln_g": 1.0 + nrm(ks[6], (DEPTH, 2, D), 0.02),
        "ln_b": nrm(ks[7], (DEPTH, 2, D), 0.02),
        "attn_w_qkv": nrm(ks[8], (N_ATTN_LAYERS, D, Q_WIDTH + 2 * KV_WIDTH), D ** -0.5) * qkv_col_scale,
        "attn_w_o": nrm(ks[9], (N_ATTN_LAYERS, Q_WIDTH, D), Q_WIDTH ** -0.5 * DEEPNORM_BETA),
        "attn_sinks": nrm(ks[10], (N_ATTN_LAYERS, N_HEADS), 0.5),
        "fnet_w": nrm(ks[11], (N_FNET_LAYERS, D, D), D ** -0.5 * DEEPNORM_BETA),
        "router_w": nrm(ks[12], (DEPTH, D, N_EXPERTS), D ** -0.5),
        "router_bias": nrm(ks[13], (DEPTH, N_EXPERTS), 0.01),
        "exp_w_gate": nrm(ks[14], (DEPTH, N_EXPERTS, D, EXPERT_FF), D ** -0.5),
        "exp_w_up": nrm(ks[15], (DEPTH, N_EXPERTS, D, EXPERT_FF), D ** -0.5),
        "exp_w_down": nrm(ks[16], (DEPTH, N_EXPERTS, EXPERT_FF, D), EXPERT_FF ** -0.5 * DEEPNORM_BETA),
        "sh_w_gate": nrm(ks[17], (DEPTH, D, SHARED_FF), D ** -0.5),
        "sh_w_up": nrm(ks[18], (DEPTH, D, SHARED_FF), D ** -0.5),
        "sh_w_down": nrm(ks[19], (DEPTH, SHARED_FF, D), SHARED_FF ** -0.5 * DEEPNORM_BETA),
    }

def reference(x, c, ctx, c_ctx, w_ada, b_ada, ln_g, ln_b, attn_w_qkv, attn_w_o, attn_sinks, fnet_w,
              router_w, router_bias, exp_w_gate, exp_w_up, exp_w_down, sh_w_gate, sh_w_up, sh_w_down):
    B, L, D = x.shape
    C = ctx.shape[1]
    cos, sin = axial_rope_tables(L)
    h = ctx
    silu_c = jax.nn.silu(c)
    silu_cc = jax.nn.silu(c_ctx)
    for i in range(DEPTH):
        kind = i % N_MIXERS
        j = i // N_MIXERS
        update_ctx = any((l % N_MIXERS) == 0 for l in range(i + 1, DEPTH))
        mod = silu_c @ w_ada[i] + b_ada[i]
        sh1, sc1, g1, sh2, sc2, g2 = [m[:, None, :] for m in jnp.split(mod, 6, axis=-1)]
        csh1, csc1, cg1, csh2, csc2, cg2 = jnp.split(silu_cc @ w_ada[i] + b_ada[i], 6, axis=-1)

        u = modulate(x, sh1, sc1)
        if kind == 0:
            uc = modulate(h, csh1, csc1)
            y, yc = attention_mixer(u, uc, attn_w_qkv[j], attn_w_o[j], attn_sinks[j], cos, sin, update_ctx)
        else:
            y = fourier_mixer(u, fnet_w[j])
            yc = fourier_mixer(modulate(h, csh1, csc1), fnet_w[j]) if update_ctx else None
        x = post_norm(x, g1 * y, ln_g[i, 0], ln_b[i, 0])
        if update_ctx:
            h = post_norm(h, cg1 * yc, ln_g[i, 0], ln_b[i, 0])

        u2 = modulate(x, sh2, sc2)
        if update_ctx:
            u2c = modulate(h, csh2, csc2)
            toks = jnp.concatenate([u2.reshape(-1, D), u2c.reshape(-1, D)], axis=0)
            f = moe_ffn(toks, router_w[i], router_bias[i], exp_w_gate[i], exp_w_up[i], exp_w_down[i],
                        sh_w_gate[i], sh_w_up[i], sh_w_down[i])
            y2 = f[:B * L].reshape(B, L, D)
            h = post_norm(h, cg2 * f[B * L:].reshape(B, C, D), ln_g[i, 1], ln_b[i, 1])
        else:
            y2 = moe_ffn(u2.reshape(-1, D), router_w[i], router_bias[i], exp_w_gate[i], exp_w_up[i],
                         exp_w_down[i], sh_w_gate[i], sh_w_up[i], sh_w_down[i]).reshape(B, L, D)
        x = post_norm(x, g2 * y2, ln_g[i, 1], ln_b[i, 1])
    return x


_drawn_inputs = setup_inputs


def setup_inputs(seed=0):
    import zlib

    import numpy as np

    out = dict(_drawn_inputs(seed))
    spreads = {}
    factors = {'attn_sinks': 8.0}
    for name, (base, spread) in spreads.items():
        noise = np.random.default_rng([zlib.crc32(name.encode()), seed]).standard_normal(out[name].shape)
        drawn = base * np.exp(spread * noise) if base else spread * noise
        out[name] = __import__('jax').numpy.asarray(drawn.astype(out[name].dtype))
    for name, factor in factors.items():
        out[name] = (out[name] * factor).astype(out[name].dtype)
    return out
```

```python
from contextlib import ExitStack, contextmanager

import numpy as np

import concourse.bass as bass
from concourse import mybir

F32 = mybir.dt.float32
BF16 = mybir.dt.bfloat16
I32 = mybir.dt.int32
U32 = mybir.dt.uint32
ALU = mybir.AluOpType
ACT = mybir.ActivationFunctionType
AX = mybir.AxisListType.X
ds = bass.ds

P = 128
D = 1024
SEQ = 1024
CTX = 256
KT = D // P
NT = SEQ // P
CT = CTX // P
HEADS, KV_HEADS, HD = 16, 4, 64
QW, KVW = HEADS * HD, KV_HEADS * HD
GRID_W = 64
WINDOW = 128
EXPERTS, TOP_K, GROUPS, TOP_GROUPS = 64, 8, 8, 4
FF = D // 4
FK = FF // P
SCALED = 2.5
DEPTH = 2
ALPHA = (2.0 * DEPTH) ** 0.25
LN_EPS, MOD_EPS = 1e-5, 1e-6
FG = 4
FGW = D // FG
RING = 4
DUMMY = SEQ
TABLE = 256
KSLOTS = NT + 2 + CT
CHUNK = 512
MODS = 6 * D // CHUNK


class Links:

    def __init__(self, eng, sem, base=0):
        self.eng, self.sem, self.base, self.n = eng, sem, base, 0

    def __call__(self, ins):
        self.n += 1
        ins.then_inc(self.sem, 1)
        self.eng.wait_ge(self.sem, self.base + self.n)


def settle(eng, sem):
    eng.sem_inc(sem, 1)


def inside(s, low, high):
    return low <= s < high if isinstance(s, int) else True


def steps(eng, count, head, tail, body):
    assert head % 2 == 0 and (count - tail) % 2 == 0
    for s in range(head):
        body(s, s % 2)
    with eng.Fori(head // 2, (count - tail) // 2) as i:
        for par in range(2):
            body(2 * i + par, par)
    for s in range(count - tail, count):
        body(s, s % 2)


def after(eng, sem, s, lag):
    if not isinstance(s, int) or s >= lag:
        eng.wait_ge(sem, s - lag + 1)


def at_least(eng, sem, value):
    if not isinstance(value, int) or value > 0:
        eng.wait_ge(sem, value)


def rounds(eng, count, body):
    body(0)
    with eng.Fori(1, count) as i:
        body(i)


def constants():
    f = np.float32
    p = np.arange(P)
    inv = f(10000.0) ** (-np.arange(0, HD // 2, 2, dtype=f) / f(HD // 2))
    row = np.repeat(np.arange(SEQ // GRID_W, dtype=f), GRID_W)[:, None] * inv
    col = np.tile(np.arange(GRID_W, dtype=f), SEQ // GRID_W)[:, None] * inv
    ang = np.concatenate([row, row, col, col], -1).astype(np.float64)
    sign = np.where((np.arange(HD) // (HD // 4)) % 2 == 0, -1.0, 1.0)
    rope = np.concatenate([np.cos(ang), np.sin(ang) * sign], -1).astype(f)
    gone = f(-1e30)
    before = np.where(p[:, None] <= p[None, :], f(0), gone)
    after = np.where(p[None, :] <= p[:, None], f(0), gone)
    none = np.full((P, P), gone, f)
    mask = np.stack([np.stack([none if t == 0 else before, none if t == NT - 1 else after], 1) for t in range(NT)], 1)
    a = 2 * np.pi * (np.outer(np.arange(FGW), np.arange(FGW)) % FGW) / FGW
    norm = 1.0 / np.sqrt(SEQ * FGW)
    feat = (np.concatenate([np.cos(a), np.sin(a)], 1) * norm).astype(f)
    k = (np.arange(NT)[:, None] + NT * p[None, :])
    b = 2 * np.pi * ((p[:, None, None] * k[None]) % SEQ) / SEQ
    tok = np.stack([np.cos(b), np.sin(b)], 2).astype(f)
    small = np.zeros((P, 16), f)
    small[:, 0] = DUMMY + p
    small[:, 1] = -(DUMMY + p)
    small[:, 2] = p
    small[:, 3] = p + P
    return {
        "rope": rope.reshape(SEQ, 2 * HD),
        "mask": mask.reshape(P, NT * 2 * P).astype(f),
        "feat": feat.reshape(FGW // P, P, 2 * FGW).transpose(1, 0, 2).reshape(P, -1).copy(),
        "tok": tok.reshape(P, NT * 2 * P).copy(),
        "tri": (p[:, None] < p[None, :]).astype(f),
        "ident": np.eye(P, dtype=f),
        "slots": np.tile((np.arange(9)[:, None] * P + p[None, :]).reshape(1, -1).astype(f), (P, 1)),
        "small": small,
    }


def trunk(nc, A, out, stop=None):
    dram = lambda name, shape, dt=F32: nc.dram_tensor(name, shape, dt).ap()
    q_dram = dram("qT_scratch", [NT, P, KT * P])
    u_dram = dram("u_scratch", [SEQ + P, D])
    y_dram = dram("y_scratch", [SEQ + P, D])
    x_dram = dram("x_scratch", [SEQ, D])
    o_dram = dram("o_scratch", [SEQ, D])
    table_dram = dram("table_scratch", [TABLE, 4], I32)

    with ExitStack() as whole:
        stages = []

        def pools(ctx):
            stages.append(None)
            tag = f"_{len(stages)}"

            def sb(name, shape, dt=F32):
                return ctx.enter_context(nc.sbuf_tensor(name + tag, shape, dt))

            def ps(name, shape, dt=F32):
                return ctx.enter_context(nc.psum_tensor(name + tag, shape, dt))

            def sem(name):
                made.append(nc.alloc_semaphore(name + tag))
                return made[-1]

            def clear():
                if made:
                    nc.clear_and_free_semaphores(made)
                    nc.all_engine_barrier()
            made = []
            ctx.callback(clear)
            return sb, ps, sem

        sb, _, sem = pools(whole)
        ident = sb("ident", [P, P])
        waited = sem("waited")
        x = sb("x", [P, NT, D])
        mod = sb("mod", [P, 6 * D])
        halves = sb("halves", [P, 1])
        ones = sb("ones", [P, P])
        shift1, scale1, gate1, shift2, scale2, gate2 = (mod[:, i * D:(i + 1) * D] for i in range(6))
        gather_sems = [[sem(f"gathered_l{l}_{i}") for i in range(2)] for l in range(DEPTH)]
        scatter_sems = [[sem(f"added_l{l}_{i}") for i in range(2)] for l in range(DEPTH)]

        def ada(layer, modc=None):
            with_ctx = layer == 0
            nv = 2 if with_ctx else 1
            with ExitStack() as ctx:
                sb, ps, sem = pools(ctx)
                ring = sb("ada_w", [P, 4, KT, CHUNK])
                bias = sb("ada_b", [1, 6 * D])
                cond = sb("cond", [P, nv, KT])
                e = sb("cond_e", [P, nv, KT])
                silu = sb("cond_silu", [P, nv, KT])
                rows = sb("cond_rows", [P, nv, KT, P])
                acc = ps("ada_acc", [P, 2, 2, CHUNK])
                w_in = [sem(f"ada_w_in{i}") for i in range(4)]
                c_in, e_done, rows_done = sem("c_in"), sem("silu_exp"), sem("rows_done")
                mm_done, out_done, own = sem("ada_mm"), sem("ada_out"), sem("ada_own")
                w = A["w_ada"][layer].rearrange("(p k) n -> p k n", k=KT)

                with nc.Block() as block:
                    @block.sync
                    def _(sp):
                        sp.dma_start(cond[:, 0, :], A["c"][0].rearrange("(p k) -> p k", k=KT)).then_inc(c_in, 16)
                        if with_ctx:
                            sp.dma_start(cond[:, 1, :], A["c_ctx"].rearrange("(p k) -> p k", k=KT)).then_inc(c_in, 16)
                            sp.dma_start(ident[:], A["ident"]).then_inc(c_in, 16)
                            sp.dma_start(x[:], A["x"][0].rearrange("(t p) d -> p t d", p=P)).then_inc(c_in, 16)
                        sp.dma_start(bias[:], A["b_ada"][layer:layer + 1]).then_inc(c_in, 16)
                        for r in range(4):
                            sp.dma_start(ring[:, r], w[:, :, r * CHUNK:(r + 1) * CHUNK]).then_inc(w_in[r], 16)
                        with sp.Fori(1, MODS // 4) as i:
                            for r in range(4):
                                sp.wait_ge(mm_done, 4 * i + r - 3)
                                sp.dma_start(ring[:, r], w[:, :, ds((4 * i + r) * CHUNK, CHUNK)]).then_inc(w_in[r], 16)

                    nload = 5 if with_ctx else 2

                    @block.scalar
                    def _(act):
                        act.wait_ge(c_in, 16 * nload)
                        act.activation(e[:], cond[:], ACT.Exp, scale=-1.0).then_inc(e_done, 1)

                    @block.vector
                    def _(dve):
                        link = Links(dve, own)
                        dve.memset(ones[:], 1.0)
                        link(dve.memset(halves[:], -0.5))
                        dve.wait_ge(e_done, 1)
                        link(dve.tensor_scalar(e[:], e[:], 1.0, None, ALU.add))
                        link(dve.reciprocal(e[:], e[:]))
                        link(dve.tensor_tensor(silu[:], cond[:], e[:], ALU.mult))
                        dve.tensor_copy(rows[:], silu[:].unsqueeze(3).to_broadcast([P, nv, KT, P])).then_inc(rows_done, 1)

                        def take(n, par, both):
                            dve.wait_ge(mm_done, n + 1)
                            if both:
                                dve.tensor_copy(modc[:, ds(n * CHUNK, CHUNK)], acc[:, par, 1, :])
                            dve.tensor_copy(mod[:, ds(n * CHUNK, CHUNK)], acc[:, par, 0, :]).then_inc(out_done, 1)
                        first = 4 if with_ctx else 0
                        for n in range(first):
                            take(n, n % 2, True)
                        with dve.Fori(first // 2, MODS // 2) as i:
                            for par in range(2):
                                take(2 * i + par, par, False)
                        dve.wait_ge(out_done, MODS)
                        dve.tensor_scalar(scale1, scale1, 1.0, None, ALU.add)
                        dve.tensor_scalar(scale2, scale2, 1.0, None, ALU.add)
                        if with_ctx:
                            dve.tensor_scalar(modc[:, D:2 * D], modc[:, D:2 * D], 1.0, None, ALU.add)

                    @block.tensor
                    def _(pe):
                        pe.wait_ge(rows_done, 1)
                        pe.wait_ge(c_in, 16 * nload)

                        def chunk(n, i, r, both):
                            pe.wait_ge(w_in[r], 16 * (i + 1))
                            if not isinstance(n, int) or n >= 2:
                                pe.wait_ge(out_done, n - 1)
                            for v in range(2 if both else 1):
                                o = acc[:, r % 2, v, :]
                                for k in range(KT):
                                    pe.matmul(o, rows[:, v, k, :], ring[:, r, k, :], start=k == 0, stop=False)
                                last = pe.matmul(o, ones[0:1, :], bias[0:1, ds(n * CHUNK, CHUNK)], start=False, stop=True)
                            last.then_inc(mm_done, 1)
                        for r in range(4):
                            chunk(r, 0, r, with_ctx)
                        with pe.Fori(1, MODS // 4) as i:
                            for r in range(4):
                                chunk(4 * i + r, i, r, False)

        def root(ctx, sem):
            sb, _, _ = pools(ctx)
            return dict(st=sb("bn", [P, 2, 6]), mv=sb("mean_var", [P, 2]), var=sb("var", [P, 1]),
                        rstd=sb("rstd", [P, 1]), asked=sem("var_ready"), ready=sem("root_ready"))

        def normalise(dve, link, r, z, out, eps, n):
            settle(dve, waited)
            dve.bn_stats(r["st"][:, 0, :], z[:, 0:512])
            link(dve.bn_stats(r["st"][:, 1, :], z[:, 512:1024]))
            settle(dve, waited)
            link(dve.bn_aggr(r["mv"][:], r["st"][:]))
            dve.tensor_scalar(r["var"][:], r["mv"][:, 1:2], eps, None, ALU.add).then_inc(r["asked"], 1)
            dve.wait_ge(r["ready"], n)
            link(dve.tensor_scalar(out, z, r["mv"][:, 0:1], r["rstd"][:], ALU.subtract, ALU.mult))

        def roots(pool, r, count):
            with pool.Fori(0, count) as n:
                pool.wait_ge(r["asked"], n + 1)
                pool.tensor_tensor(r["rstd"][:], r["var"][:], halves[:], ALU.pow).then_inc(r["ready"], 1)

        def tile(buf, t):
            return buf[:, ds(t, 1), :].rearrange("p a d -> p (a d)")

        def project_qkv(kT, v, modc):
            with ExitStack() as ctx:
                sb, ps, sem = pools(ctx)
                w = sb("w_qkv", [P, KT, QW + 2 * KVW])
                cx = sb("cx", [P, CT, D])
                u = sb("u", [P, 2, D])
                uT = sb("uT", [P, 2, KT, P])
                qk = sb("qk", [P, QW + KVW])
                t1 = sb("t1", [P, QW + KVW])
                t2 = sb("t2", [P, QW + KVW])
                kr = sb("kr", [P, KV_HEADS, 2, HD])
                qT = sb("qT", [P, 2, KT, P])
                rope = sb("rope", [P, NT, 2 * HD])
                r = root(ctx, sem)
                psT = ps("psT", [P, KT, P])
                psQ = ps("psQ", [P, 3, 512])
                psqT = ps("psqT", [P, KT, P])
                pskT = ps("pskT", [P, KV_HEADS, P])
                w_in = sem("wqkv_in")
                mod_own, rope_own, zeroed = sem("mod_own"), sem("rope_own"), sem("zeroed")
                u_done, uT_mm, uT_done = sem("u_done"), sem("uT_mm"), sem("uT_done")
                mm_done, qk_done, rope_done = sem("qkv_mm"), sem("qk_copied"), sem("rope_done")
                T_done, qT_done, kT_done = sem("qkT_mm"), sem("qT_done"), sem("kT_done")
                q_out = [sem(f"q_out{i}") for i in range(2)]
                N = CT + NT
                count, head, tail = N + 2, CT + 4, 2
                zeros = 4

                with nc.Block() as block:
                    @block.sync
                    def _(sp):
                        sp.dma_start(cx[:], A["ctx"][0].rearrange("(t p) d -> p t d", p=P)).then_inc(w_in, 16)
                        sp.dma_start(rope[:], A["rope"].rearrange("(t p) c -> p t c", p=P)).then_inc(w_in, 16)
                        sp.dma_start(w[:], A["attn_w_qkv"][0].rearrange("(k p) n -> p k n", p=P)).then_inc(w_in, 16)
                        with sp.Fori(0, NT // 2) as i:
                            for par in range(2):
                                sp.wait_ge(qT_done, 2 * i + par + 1)
                                sp.dma_start(q_dram[ds(2 * i + par, 1)].rearrange("a p c -> (a p) c"),
                                             qT[:, par].rearrange("p k c -> p (k c)")).then_inc(q_out[par], 16)
                        for par in range(2):
                            sp.wait_ge(q_out[par], 16 * (NT // 2))

                    @block.gpsimd
                    def _(pool):
                        roots(pool, r, N)

                    @block.vector
                    def _(dve):
                        for s in (0, NT + 1):
                            dve.memset(kT[:, :, s * P:(s + 1) * P], 0.0)
                            dve.memset(v[:, s, :], 0.0)
                        dve.wait_ge(w_in, 48)

                        def modulate(s, par, src, sh, sc):
                            link = Links(dve, mod_own, s * 4)
                            after(dve, uT_mm, s, 2)
                            uu = u[:, par, :]
                            normalise(dve, link, r, src, uu, MOD_EPS, s + 1)
                            link(dve.tensor_tensor(uu, uu, sc, ALU.mult))
                            dve.tensor_tensor(uu, uu, sh, ALU.add).then_inc(u_done, 1)
                            assert link.n == 4

                        def rotate(s, t):
                            link = Links(dve, rope_own, t * 1)
                            dve.wait_ge(qk_done, s + 1)
                            after(dve, T_done, s, 1)
                            n = HEADS + KV_HEADS
                            cs = rope[:, ds(t, 1), 0:HD].to_broadcast([P, n, HD])
                            sn = rope[:, ds(t, 1), HD:2 * HD].rearrange("p a (x b c) -> p a x b c", b=2, c=HD // 4)
                            dve.tensor_tensor(t1[:].rearrange("p (h d) -> p h d", d=HD),
                                              qk[:].rearrange("p (h d) -> p h d", d=HD), cs, ALU.mult)
                            src = qk[:].rearrange("p (h x b c) -> p h x b c", x=2, b=2, c=HD // 4)
                            dst = t2[:].rearrange("p (h x b c) -> p h x b c", x=2, b=2, c=HD // 4)
                            for half in range(2):
                                for b in range(2):
                                    last = dve.tensor_tensor(dst[:, :, half, b, :], src[:, :, half, 1 - b, :],
                                                             sn[:, :, half, b, :].to_broadcast([P, n, HD // 4]), ALU.mult)
                            link(last)
                            dve.tensor_tensor(t1[:, 0:QW], t1[:, 0:QW], t2[:, 0:QW], ALU.add)
                            twice = lambda b: b[:, QW:].rearrange("p (h d) -> p h d", d=HD).unsqueeze(2).to_broadcast([P, KV_HEADS, 2, HD])
                            dve.tensor_tensor(kr[:], twice(t1), twice(t2), ALU.add).then_inc(rope_done, 1)

                        def body(s, par):
                            if inside(s, 0, N):
                                if isinstance(s, int) and s < CT:
                                    modulate(s, par, cx[:, s], modc[:, 0:D], modc[:, D:])
                                else:
                                    modulate(s, par, tile(x, s - CT), shift1, scale1)
                            if inside(s - 2, 0, N):
                                dve.wait_ge(T_done, s - 1)
                                slot = s - 2 + NT + 2 if isinstance(s, int) and s - 2 < CT else s - 2 - CT + 1
                                dve.tensor_copy(kT[:, :, ds(slot * P, P)], pskT[:]).then_inc(kT_done, 1)
                            if inside(s - 1, 0, N):
                                if isinstance(s, int) and s - 1 < CT:
                                    dve.wait_ge(qk_done, s)
                                    after(dve, T_done, s - 1, 1)
                                    kk = qk[:, QW:].rearrange("p (h d) -> p h d", d=HD)
                                    dve.tensor_copy(kr[:], kk.unsqueeze(2).to_broadcast([P, KV_HEADS, 2, HD])).then_inc(rope_done, 1)
                                else:
                                    rotate(s - 1, s - 1 - CT)
                        steps(dve, count, head, tail, body)

                    @block.scalar
                    def _(act):
                        def body(s, par):
                            if inside(s, 0, N):
                                act.wait_ge(uT_mm, s + 1)
                                after(act, mm_done, s, 2)
                                act.activation(uT[:, par], psT[:], ACT.Copy).then_inc(uT_done, 1)
                            context = isinstance(s, int)
                            if inside(s - 1, 0, N):
                                is_ctx = isinstance(s, int) and s - 1 < CT
                                act.wait_ge(mm_done, s)
                                slot = s - 1 + NT + 2 if is_ctx else s - 1 - CT + 1
                                act.activation(tile(v, slot), psQ[:, 2, KVW:], ACT.Copy)
                                after(act, rope_done, s - 1, 1)
                                if not is_ctx:
                                    act.activation(qk[:, 0:QW], psQ[:, 0:2].rearrange("p a b -> p (a b)"), ACT.Copy)
                                act.activation(qk[:, QW:], psQ[:, 2, 0:KVW], ACT.Copy).then_inc(qk_done, 1)
                            if inside(s - 2, CT, N):
                                t = s - 2 - CT
                                act.wait_ge(T_done, s - 1)
                                at_least(act, q_out[par], (t - par) * 8)
                                act.activation(qT[:, par], psqT[:], ACT.Copy).then_inc(qT_done, 1)
                        steps(act, count, head, tail, body)

                    @block.tensor
                    def _(pe):
                        def body(s, par):
                            if inside(s - 1, 0, N):
                                is_ctx = isinstance(s, int) and s - 1 < CT
                                pe.wait_ge(uT_done, s)
                                pe.wait_ge(w_in, 48)
                                after(pe, qk_done, s - 1, 1)
                                for c in (2,) if is_ctx else range(3):
                                    for k in range(KT):
                                        last = pe.matmul(psQ[:, c], uT[:, 1 - par, k], w[:, k, c * 512:(c + 1) * 512],
                                                         start=k == 0, stop=k == KT - 1)
                                last.then_inc(mm_done, 1)
                            if inside(s, 0, N):
                                pe.wait_ge(u_done, s + 1)
                                after(pe, uT_done, s, 1)
                                for k in range(KT):
                                    last = pe.transpose(psT[:, k], u[:, par, k * P:(k + 1) * P], ident[:])
                                last.then_inc(uT_mm, 1)
                            if inside(s - 2, 0, N):
                                is_ctx = isinstance(s, int) and s - 2 < CT
                                pe.wait_ge(rope_done, s - 1)
                                after(pe, kT_done, s - 2, 1)
                                if not is_ctx:
                                    after(pe, qT_done, s - 2 - CT, 1)
                                    for k in range(KT):
                                        pe.transpose(psqT[:, k], t1[:, k * P:(k + 1) * P], ident[:])
                                for h in range(KV_HEADS):
                                    last = pe.transpose(pskT[:, h], kr[:, h].rearrange("p a d -> p (a d)"), ident[:])
                                last.then_inc(T_done, 1)
                        steps(pe, count, head, tail, body)

        def attend(kT, v):
            W = 3 * P
            SC = HD ** -0.5
            H, SLOTS = HEADS, 4
            S0 = 512 - W
            O0 = 512 + CTX
            with ExitStack() as ctx:
                sb, ps, sem = pools(ctx)
                qT = sb("qT_in", [P, 2, 2, KT, P])
                halves_of = (slice(0, HD), slice(HD, P))
                o = sb("o", [P, 2, D])
                maskf = sb("mask_f", [P, NT, 2, P])
                mask = sb("mask", [P, NT, 2, P], BF16)
                identb = sb("identb", [P, P], BF16)
                sink, nsink = sb("sink", [P, HEADS]), sb("nsink", [P, HEADS])
                mx, nm = sb("mx", [P, HEADS]), sb("nm", [P, 2, HEADS])
                rs, es, den = sb("row_sum", [P, 2, HEADS]), sb("sink_exp", [P, HEADS]), sb("den", [P, HEADS])
                prob = sb("prob", [P, 2, W + CTX])
                pT = sb("pT", [P, 2, W + CTX])
                bank = [ps(f"head{i}", [P, 1024]) for i in range(SLOTS)]
                c_in, set_up, own = sem("att_in"), sem("att_set_up"), sem("att_own")
                q_in = [sem(f"q_in{i}") for i in range(2)]
                o_out = [sem(f"o_out{i}") for i in range(2)]
                q_zeros, score_mm, max_done, exp_done = sem("q_zeros"), sem("score_mm"), sem("max_done"), sem("exp_done")
                T_mm, copied_a, copied_d, pv_mm, o_done = (sem(n) for n in ("probT_mm", "probT_a", "probT_d", "pv_mm", "o_done"))
                sink_in, sink_done, den_done, tile_done = (sem(n) for n in ("sink_in", "sink_done", "den_done", "tile_done"))
                keys = [(0, P), (P, 2 * P), (2 * P, W), (W, W + P), (W + P, W + CTX)]

                def each(eng, body):
                    steps(eng, NT, 2, 2, body)

                def past(eng, sem, g, lag):
                    if not isinstance(g, int) or g >= lag:
                        eng.wait_ge(sem, g - lag + 1)

                def ahead(t, par, h, lead):
                    if h + lead < H:
                        return t, par, h + lead
                    if isinstance(t, int) and t == NT - 1:
                        return None
                    return t + 1, 1 - par, h + lead - H

                def behind(t, par, h):
                    if h > 0:
                        return t, par, h - 1
                    if isinstance(t, int) and t == 0:
                        return None
                    return t - 1, 1 - par, H - 1

                with nc.Block() as block:
                    @block.sync
                    def _(sp):
                        sp.dma_start(maskf[:].rearrange("p t a b -> p (t a b)"), A["mask"]).then_inc(c_in, 16)
                        sp.dma_start(sink[:], A["attn_sinks"][0:1].to_broadcast([P, HEADS])).then_inc(c_in, 16)

                        def load(t, par):
                            for odd, rows in enumerate(halves_of):
                                sp.dma_start(qT[rows, par, odd].rearrange("p k c -> p (k c)"),
                                             q_dram[ds(t, 1), rows].rearrange("a p c -> (a p) c")).then_inc(q_in[par], 16)

                        def store(t, par):
                            sp.wait_ge(tile_done, t + 1)
                            sp.dma_start(o_dram[ds(t * P, P), :], o[:, par]).then_inc(o_out[par], 16)
                        load(0, 0)
                        load(1, 1)
                        with sp.Fori(1, NT // 2) as i:
                            for par in range(2):
                                sp.wait_ge(score_mm, (2 * i + par - 1) * H)
                                load(2 * i + par, par)
                                store(2 * i + par - 2, par)
                        for par in range(2):
                            store(NT - 2 + par, par)
                        for par in range(2):
                            sp.wait_ge(o_out[par], 16 * (NT // 2))

                    @block.gpsimd
                    def _(pool):
                        for odd, rows in enumerate(reversed(halves_of)):
                            pool.memset(qT[rows, :, odd], 0.0).then_inc(q_zeros, 1)

                        def divide(t, par):
                            pool.wait_ge(den_done, t + 1)
                            pool.wait_ge(o_done, (t + 1) * H)
                            rows = o[:, par].rearrange("p (h d) -> p h d", d=HD)
                            pool.tensor_tensor(rows, rows, den[:].unsqueeze(2).to_broadcast([P, H, HD]),
                                               ALU.mult).then_inc(tile_done, 1)

                        def body(t, par):
                            if inside(t, 1, NT):
                                divide(t - 1, 1 - par)
                        each(pool, body)
                        divide(NT - 1, 1)

                    @block.vector
                    def _(dve):
                        dve.wait_ge(c_in, 32)
                        dve.tensor_copy(mask[:], maskf[:]).then_inc(set_up, 1)
                        dve.tensor_copy(identb[:], ident[:]).then_inc(set_up, 1)
                        dve.tensor_scalar(nsink[:], sink[:], -1.0, None, ALU.mult).then_inc(set_up, 1)
                        dve.wait_ge(set_up, 3)

                        def top(t, par, h):
                            g = t * H + h
                            link = Links(dve, own, g)
                            dve.wait_ge(score_mm, g + 1)
                            link(dve.tensor_reduce(mx[:, h:h + 1], bank[h % SLOTS][:, S0:S0 + W + CTX], AX, ALU.max))
                            dve.scalar_tensor_tensor(out=nm[:, par, h:h + 1], in0=mx[:, h:h + 1], scalar=-SC,
                                                     in1=nsink[:, h:h + 1], op0=ALU.mult, op1=ALU.min).then_inc(max_done, 1)

                        def sinks(t, par):
                            dve.wait_ge(max_done, (t + 1) * H)
                            dve.wait_ge(exp_done, (t + 1) * H)
                            after(dve, den_done, t, 1)
                            dve.tensor_tensor(es[:], sink[:], nm[:, par], ALU.add).then_inc(sink_in, 1)

                        def denominators(t, par):
                            dve.wait_ge(sink_done, t + 1)
                            after(dve, tile_done, t, 1)
                            dve.tensor_tensor(es[:], rs[:, par], es[:], ALU.add).then_inc(sink_in, 1)
                            dve.wait_ge(sink_in, 2 * t + 2)
                            dve.reciprocal(den[:], es[:]).then_inc(den_done, 1)

                        def body(t, par):
                            for h in range(H):
                                g = t * H + h
                                dve.wait_ge(T_mm, g + 1)
                                past(dve, pv_mm, g, 2)
                                dve.tensor_copy(pT[:, h % 2, W:], bank[h % SLOTS][:, 512:512 + CTX]).then_inc(copied_d, 1)
                                nxt = ahead(t, par, h, 2)
                                if nxt:
                                    top(*nxt)
                                if inside(t, 1, NT):
                                    if h == 3:
                                        sinks(t - 1, 1 - par)
                                    if h == 6:
                                        denominators(t - 1, 1 - par)
                        top(0, 0, 0)
                        top(0, 0, 1)
                        each(dve, body)
                        sinks(NT - 1, 1)
                        denominators(NT - 1, 1)

                    @block.scalar
                    def _(act):
                        def exps(t, par, h):
                            g = t * H + h
                            act.wait_ge(max_done, g + 1)
                            past(act, T_mm, g, 2)
                            if not isinstance(t, int) or t >= 2:
                                act.wait_ge(den_done, t - 1)
                            act.activation(prob[:, h % 2], bank[h % SLOTS][:, S0:S0 + W + CTX], ACT.Exp, scale=SC,
                                           bias=nm[:, par, h:h + 1], accum_out=rs[:, par, h:h + 1]).then_inc(exp_done, 1)

                        def take(t, par, h):
                            act.wait_ge(pv_mm, t * H + h + 1)
                            if h == 0 and (not isinstance(t, int) or t >= 2):
                                act.wait_ge(o_out[par], (t - par) * 8)
                            act.activation(o[:, par, h * HD:(h + 1) * HD], bank[h % SLOTS][:, O0:O0 + HD],
                                           ACT.Copy).then_inc(o_done, 1)

                        def sinks(t):
                            act.wait_ge(sink_in, 2 * t + 1)
                            act.activation(es[:], es[:], ACT.Exp).then_inc(sink_done, 1)

                        def body(t, par):
                            for h in range(H):
                                g = t * H + h
                                nxt = ahead(t, par, h, 1)
                                if nxt:
                                    exps(*nxt)
                                act.wait_ge(T_mm, g + 1)
                                past(act, pv_mm, g, 2)
                                act.activation(pT[:, h % 2, 0:W], bank[h % SLOTS][:, S0:512], ACT.Copy).then_inc(copied_a, 1)
                                last = behind(t, par, h)
                                if last:
                                    take(*last)
                                if h == 4 and inside(t, 1, NT):
                                    sinks(t - 1)
                        exps(0, 0, 0)
                        each(act, body)
                        take(NT - 1, 1, H - 1)
                        sinks(NT - 1)

                    @block.tensor
                    def _(pe):
                        pe.wait_ge(set_up, 3)
                        pe.wait_ge(q_zeros, 2)

                        def masked(t, side):
                            return mask[:, ds(t, 1), side].rearrange("p a c -> p (a c)")

                        def scores(t, par, h):
                            g = t * H + h
                            if h == 0:
                                pe.wait_ge(q_in[par], (t - par) * 16 + 32)
                            past(pe, o_done, g, SLOTS)
                            kv = h // (HEADS // KV_HEADS)
                            q = qT[:, par, h % 2, h // 2, :]
                            sc = bank[h % SLOTS]
                            pe.matmul(sc[:, S0:512], q, kT[:, kv, ds(t * P, W)], start=True, stop=False)
                            pe.matmul(sc[:, S0:S0 + P], identb[:], masked(t, 0), start=False, stop=False)
                            pe.matmul(sc[:, S0 + 2 * P:512], identb[:], masked(t, 1), start=False, stop=True)
                            pe.matmul(sc[:, 512:512 + CTX], q, kT[:, kv, (NT + 2) * P:], start=True, stop=True).then_inc(score_mm, 1)

                        def values(t, par, h):
                            g = t * H + h
                            pe.wait_ge(copied_a, g + 1)
                            pe.wait_ge(copied_d, g + 1)
                            kv = h // (HEADS // KV_HEADS)
                            for j, (a, b) in enumerate(keys):
                                slot = t + j if j < 3 else NT + 2 + j - 3
                                rhs = v[:, ds(slot, 1), kv * HD:(kv + 1) * HD].rearrange("p a d -> p (a d)")
                                last = pe.matmul(bank[h % SLOTS][:, O0:O0 + HD], pT[:, h % 2, a:b], rhs,
                                                 start=j == 0, stop=j == len(keys) - 1)
                            last.then_inc(pv_mm, 1)

                        def body(t, par):
                            for h in range(H):
                                pe.wait_ge(exp_done, t * H + h + 1)
                                for a, b in keys:
                                    last = pe.transpose(bank[h % SLOTS][:, S0 + a:S0 + b], prob[:, h % 2, a:b], ident[:])
                                last.then_inc(T_mm, 1)
                                nxt = ahead(t, par, h, 2)
                                if nxt:
                                    scores(*nxt)
                                last = behind(t, par, h)
                                if last:
                                    values(*last)
                        scores(0, 0, 0)
                        scores(0, 0, 1)
                        each(pe, body)
                        values(NT - 1, 1, H - 1)

        def post_norm(dve, link, r, y, z, res, out, gate, lnp, n):
            link(dve.tensor_tensor(z, y, gate, ALU.mult))
            link(dve.scalar_tensor_tensor(out=z, in0=res, scalar=ALPHA, in1=z, op0=ALU.mult, op1=ALU.add))
            normalise(dve, link, r, z, z, LN_EPS, n)
            link(dve.tensor_tensor(z, z, lnp[:, 0], ALU.mult))
            return dve.tensor_tensor(out, z, lnp[:, 1], ALU.add)

        def mix(layer, src, turned, w_mix, logits):
            with ExitStack() as ctx:
                sb, ps, sem = pools(ctx)
                w = sb("w_mix", [P, KT, D])
                wr = sb("w_router", [P, KT, EXPERTS])
                wg, wu = sb("sh_gate", [P, KT, FF]), sb("sh_up", [P, KT, FF])
                wd = sb("sh_down", [P, FK, D])
                lnp = sb("lnp1", [P, 2, D])
                stage = sb("stage", [P, 2, D])
                aT = sb("aT", [P, KT, P])
                z = sb("z", [P, D])
                u = sb("u2", [P, 2, D])
                uT = sb("u2T", [P, KT, P])
                e = sb("sh_e", [P, FF])
                hid = sb("sh_h", [P, FF])
                hT = sb("sh_hT", [P, FK, P])
                yo = sb("sh_y", [P, D])
                r = root(ctx, sem)
                psT = ps("mixT", [P, KT, P])
                psY = ps("mixY", [P, 2, 512])
                psG = ps("mixG", [P, 2, FF])
                psR = ps("mixR", [P, 512])
                psD = ps("mixD", [P, 2, 512])
                w_in, own, hown = sem("mix_w_in"), sem("mix_own"), sem("sh_own")
                staged, aT_mm, aT_done, y_mm, u_done = (sem(n) for n in ("staged", "aT_mm", "aT_done", "y_mm", "u2_done"))
                uT_mm, uT_done, g_mm, e_done, h_done = (sem(n) for n in ("u2T_mm", "u2T_done", "g_mm", "sh_e_done", "sh_h_done"))
                hT_mm, hT_done, d_mm, yo_done = (sem(n) for n in ("hT_mm", "hT_done", "d_mm", "yo_done"))
                stage_in = [sem(f"stage_in{i}") for i in range(2)]
                dummy = sem("dummy_ready")
                u_out, yo_out = [sem(f"u_out{i}") for i in range(2)], sem("yo_out")
                count, head, tail = NT + 2, 4, 2
                WIN = 16 * 7

                with nc.Block() as block:
                    @block.sync
                    def _(sp):
                        sp.dma_start(w[:], w_mix.rearrange("(k p) n -> p k n", p=P)).then_inc(w_in, 16)
                        for j, name in enumerate(("ln_g", "ln_b")):
                            sp.dma_start(lnp[:, j], A[name][layer, 0:1].to_broadcast([P, D])).then_inc(w_in, 16)
                        sp.dma_start(wr[:], A["router_w"][layer].rearrange("(p k) n -> p k n", k=KT)).then_inc(w_in, 16)
                        sp.dma_start(wg[:], A["sh_w_gate"][layer].rearrange("(p k) n -> p k n", k=KT)).then_inc(w_in, 16)
                        sp.dma_start(wu[:], A["sh_w_up"][layer].rearrange("(p k) n -> p k n", k=KT)).then_inc(w_in, 16)
                        sp.dma_start(wd[:], A["sh_w_down"][layer].rearrange("(p k) n -> p k n", k=FK)).then_inc(w_in, 16)

                        def body(s, par):
                            if inside(s, 0, NT) and not turned:
                                if not isinstance(s, int) or s >= 2:
                                    sp.wait_ge(aT_mm, s - 1)
                                sp.dma_start(stage[:, par], src[ds(s * P, P), :]).then_inc(stage_in[par], 16)
                            if inside(s - 2, 0, NT):
                                t = s - 2
                                sp.wait_ge(u_done, t + 1)
                                sp.dma_start(u_dram[ds(t * P, P), :], u[:, par]).then_inc(u_out[par], 16)
                                sp.wait_ge(yo_done, t + 1)
                                sp.dma_start(y_dram[ds(t * P, P), :], yo[:]).then_inc(yo_out, 16)
                                sp.wait_ge(yo_out, 16 * (t + 1))
                                settle(sp, waited)
                        steps(sp, count, head, tail, body)
                        sp.wait_ge(dummy, 1)
                        sp.dma_start(u_dram[DUMMY:, :], yo[:]).then_inc(u_out[0], 16)
                        sp.dma_start(y_dram[DUMMY:, :], yo[:]).then_inc(yo_out, 16)
                        sp.wait_ge(yo_out, 16 * (NT + 1))
                        sp.wait_ge(u_out[0], 16 * (NT // 2 + 1))
                        sp.wait_ge(u_out[1], 16 * (NT // 2))

                    @block.gpsimd
                    def _(pool):
                        def body(t):
                            if turned:
                                at_least(pool, y_mm, t)
                                pool.tensor_copy(aT[:], src[:, :, ds(t * P, P)]).then_inc(staged, 1)
                            for j in range(2):
                                pool.wait_ge(r["asked"], 2 * t + j + 1)
                                pool.tensor_tensor(r["rstd"][:], r["var"][:], halves[:], ALU.pow).then_inc(r["ready"], 1)
                        rounds(pool, NT, body)

                    @block.vector
                    def _(dve):
                        def body(s, par):
                            if inside(s, 0, NT):
                                link = Links(dve, own, s * 11)
                                after(dve, u_done, s, 1)
                                dve.wait_ge(y_mm, s + 1)
                                xs = tile(x, s)
                                link(post_norm(dve, link, r, psY[:].rearrange("p a b -> p (a b)"), z[:], xs, xs, gate1, lnp, 2 * s + 1))
                                normalise(dve, link, r, xs, z[:], MOD_EPS, 2 * s + 2)
                                dst = u[:, par].rearrange("t (k p) -> t p k", k=KT)
                                zz = z[:].rearrange("t (p k) -> t p k", k=KT)
                                link(dve.tensor_tensor(z[:], z[:], scale2, ALU.mult))
                                after(dve, uT_mm, s, 2)
                                if not isinstance(s, int) or s >= 2:
                                    dve.wait_ge(u_out[par], (s - par) * 8)
                                dve.tensor_tensor(dst, zz, shift2.rearrange("t (p k) -> t p k", k=KT), ALU.add).then_inc(u_done, 1)
                                assert link.n == 11, link.n
                            if inside(s - 1, 0, NT):
                                link = Links(dve, hown, (s - 1) * 3)
                                dve.wait_ge(e_done, s)
                                link(dve.tensor_scalar(e[:], e[:], 1.0, None, ALU.add))
                                link(dve.reciprocal(e[:], e[:]))
                                link(dve.tensor_tensor(e[:], psG[:, 0], e[:], ALU.mult))
                                after(dve, hT_mm, s - 1, 1)
                                dve.tensor_tensor(hid[:].rearrange("t (k p) -> t p k", k=FK),
                                                  e[:].rearrange("t (p k) -> t p k", k=FK),
                                                  psG[:, 1].rearrange("t (p k) -> t p k", k=FK), ALU.mult).then_inc(h_done, 1)
                        dve.wait_ge(w_in, WIN)
                        steps(dve, count, head, tail, body)
                        dve.wait_ge(yo_out, 16 * NT)
                        dve.memset(yo[:], 0.0).then_inc(dummy, 1)

                    @block.scalar
                    def _(act):
                        def body(s, par):
                            if inside(s, 0, NT) and not turned:
                                act.wait_ge(aT_mm, s + 1)
                                after(act, y_mm, s, 1)
                                act.activation(aT[:], psT[:], ACT.Copy).then_inc(aT_done, 1)
                            if inside(s - 1, 0, NT):
                                act.wait_ge(uT_mm, s)
                                after(act, g_mm, s - 1, 1)
                                act.activation(uT[:], psT[:], ACT.Copy).then_inc(uT_done, 1)
                            if inside(s - 2, 0, NT):
                                act.wait_ge(hT_mm, s - 1)
                                after(act, d_mm, s - 2, 1)
                                act.activation(hT[:].rearrange("p k c -> p (k c)"), psR[:, 256:512], ACT.Copy).then_inc(hT_done, 1)
                                act.wait_ge(d_mm, s - 1)
                                if not isinstance(s, int) or s - 2 >= 1:
                                    act.wait_ge(yo_out, 16 * (s - 2))
                                act.activation(yo[:], psD[:].rearrange("p a b -> p (a b)"), ACT.Copy).then_inc(yo_done, 1)
                            if inside(s - 1, 0, NT):
                                act.wait_ge(g_mm, s)
                                after(act, h_done, s - 1, 1)
                                act.activation(tile(logits, s - 1), psR[:, 0:EXPERTS], ACT.Copy)
                                act.activation(e[:], psG[:, 0], ACT.Exp, scale=-1.0).then_inc(e_done, 1)
                        steps(act, count, head, tail, body)

                    @block.tensor
                    def _(pe):
                        pe.wait_ge(w_in, WIN)

                        def body(s, par):
                            if inside(s, 0, NT):
                                if turned:
                                    pe.wait_ge(staged, s + 1)
                                else:
                                    pe.wait_ge(stage_in[par], (s - par) * 8 + 16)
                                    after(pe, uT_done, s, 2)
                                    for k in range(KT):
                                        last = pe.transpose(psT[:, k], stage[:, par, k * P:(k + 1) * P], ident[:])
                                    last.then_inc(aT_mm, 1)
                                    pe.wait_ge(aT_done, s + 1)
                                if not isinstance(s, int) or s >= 1:
                                    pe.wait_ge(own, 11 * (s - 1) + 1)
                                for c in range(2):
                                    for k in range(KT):
                                        last = pe.matmul(psY[:, c], aT[:, k], w[:, k, c * 512:(c + 1) * 512],
                                                         start=k == 0, stop=k == KT - 1)
                                last.then_inc(y_mm, 1)
                            if inside(s - 1, 0, NT):
                                pe.wait_ge(u_done, s)
                                if turned:
                                    after(pe, uT_done, s - 1, 1)
                                for k in range(KT):
                                    last = pe.transpose(psT[:, k], u[:, 1 - par, k * P:(k + 1) * P], ident[:])
                                last.then_inc(uT_mm, 1)
                            if inside(s - 2, 0, NT):
                                pe.wait_ge(h_done, s - 1)
                                for k in range(FK):
                                    last = pe.transpose(psR[:, 256 + k * P:256 + (k + 1) * P], hid[:, k * P:(k + 1) * P], ident[:])
                                last.then_inc(hT_mm, 1)
                                pe.wait_ge(hT_done, s - 1)
                                after(pe, yo_done, s - 2, 1)
                                for c in range(2):
                                    for k in range(FK):
                                        last = pe.matmul(psD[:, c], hT[:, k], wd[:, k, c * 512:(c + 1) * 512],
                                                         start=k == 0, stop=k == FK - 1)
                                last.then_inc(d_mm, 1)
                            if inside(s - 1, 0, NT):
                                pe.wait_ge(uT_done, s)
                                after(pe, e_done, s - 1, 1)
                                after(pe, h_done, s - 1, 1)
                                for k in range(KT):
                                    pe.matmul(psR[:, 0:EXPERTS], uT[:, k], wr[:, k], start=k == 0, stop=k == KT - 1)
                                for k in range(KT):
                                    pe.matmul(psG[:, 0], uT[:, k], wg[:, k], start=k == 0, stop=k == KT - 1)
                                for k in range(KT):
                                    last = pe.matmul(psG[:, 1], uT[:, k], wu[:, k], start=k == 0, stop=k == KT - 1)
                                last.then_inc(g_mm, 1)
                        steps(pe, count, head, tail, body)

        def route(layer, logits, place, moving, table, pends, w_all):
            with ExitStack() as ctx:
                sb, ps, sem = pools(ctx)
                E = EXPERTS
                bias = sb("r_bias", [P, E])
                small = sb("r_small", [P, 16])
                trif, tri, onesb = sb("trif", [P, P]), sb("tri", [P, P], BF16), sb("onesb", [P, P], BF16)
                sc, sel = sb("r_score", [P, NT, E]), sb("r_sel", [P, NT, E])
                t8, g8 = sb("r_top", [P, NT, GROUPS, 8]), sb("r_gtop", [P, NT, 8])
                gs, gr, gm = sb("r_gs", [P, NT, GROUPS]), sb("r_gr", [P, NT, GROUPS]), sb("r_gm", [P, NT, GROUPS])
                rep = sb("r_rep", [P, NT, E])
                m = sb("r_mask", [P, NT, E])
                mb, cb = sb("r_maskb", [P, NT, E], BF16), sb("r_cumb", [P, NT + 1, E], BF16)
                wt = sb("r_w", [P, NT, E])
                part, rest = sb("r_part", [P, NT, E], BF16), sb("r_rest", [P, NT, E])
                tot = sb("r_tot", [P, NT])
                cnt, nblk, pend = sb("r_cnt", [P, E]), sb("r_nblk", [P, E]), sb("r_pend", [P, E])
                ks, cmp8 = sb("r_ks", [P, 8]), sb("r_cmp8", [P, E, 8])
                le, lep = sb("r_le", [P, E]), sb("r_lep", [P, E])
                eb, kb, fb = sb("r_eb", [P, 2]), sb("r_kb", [P, 2]), sb("r_fb", [P, 2])
                rowf, rowi = sb("r_rowf", [P, 2, 4]), sb("r_rowi", [P, 2, 4], I32)
                psP, psC = ps("r_place", [P, NT * E]), ps("r_count", [P, E])
                c_in, own, e_done, mask_done, mm_done, iota_done = (sem(n) for n in (
                    "r_in", "r_own", "r_exp", "r_mask_done", "r_mm", "r_iota"))
                rows_done, rows_out, table_in = sem("r_rows"), sem("r_rows_out"), sem("r_table_in")
                GONE = -3.0e38

                with nc.Block() as block:
                    @block.sync
                    def _(sp):
                        sp.dma_start(bias[:], A["router_bias"][layer:layer + 1].to_broadcast([P, E])).then_inc(c_in, 16)
                        sp.dma_start(small[:], A["small"]).then_inc(c_in, 16)
                        sp.dma_start(trif[:], A["tri"]).then_inc(c_in, 16)
                        sp.wait_ge(rows_done, 1)
                        sp.dma_start(table_dram.rearrange("(a p) c -> p a c", p=P), rowi[:]).then_inc(rows_out, 16)
                        sp.wait_ge(rows_out, 16)
                        sp.dma_start(table[:], table_dram.rearrange("(o b) c -> o (b c)", o=1)).then_inc(table_in, 16)
                        sp.wait_ge(table_in, 16)

                    @block.gpsimd
                    def _(pool):
                        pool.iota(moving[:, :, :, 0], [[P, NT], [0, E]], base=0, channel_multiplier=0,
                                  allow_small_or_imprecise_dtypes=True)
                        pool.iota(moving[:, :, :, 1], [[0, NT], [0, E]], base=0, channel_multiplier=1,
                                  allow_small_or_imprecise_dtypes=True)
                        pool.iota(moving[:, :, :, 2], [[0, NT], [0, E]], base=1, channel_multiplier=0,
                                  allow_small_or_imprecise_dtypes=True)
                        pool.iota(ks[:], [[P, 8]], base=0, channel_multiplier=0,
                                  allow_small_or_imprecise_dtypes=True).then_inc(iota_done, 1)

                    @block.scalar
                    def _(act):
                        act.activation(sc[:], logits[:], ACT.Exp, scale=-1.0).then_inc(e_done, 1)

                    @block.tensor
                    def _(pe):
                        pe.wait_ge(mask_done, 1)
                        pe.matmul(psP[:], tri[:], mb[:].rearrange("p t e -> p (t e)"), start=True, stop=False)
                        pe.matmul(psP[:], onesb[:], cb[:, 0:NT].rearrange("p t e -> p (t e)"), start=False, stop=True)
                        pe.matmul(psC[:], onesb[:], cb[:, NT], start=True, stop=True).then_inc(mm_done, 1)

                    @block.vector
                    def _(dve):
                        link = Links(dve, own)
                        tt, ts = dve.tensor_tensor, dve.tensor_scalar
                        dve.wait_ge(e_done, 1)
                        dve.wait_ge(c_in, 48)
                        dve.tensor_copy(tri[:], trif[:])
                        dve.memset(onesb[:], 1.0)
                        dve.memset(cb[:, 0], 0.0)
                        link(ts(sc[:], sc[:], 1.0, None, ALU.add))
                        link(dve.reciprocal(sc[:], sc[:]))
                        link(tt(sel[:], sc[:], bias[:].unsqueeze(1).to_broadcast([P, NT, E]), ALU.add))
                        per = E // GROUPS
                        for t in range(NT):
                            for g in range(GROUPS):
                                last = dve.max(t8[:, t, g], sel[:, t, g * per:(g + 1) * per])
                        link(last)
                        link(tt(gs[:], t8[:, :, :, 0], t8[:, :, :, 1], ALU.add))
                        for t in range(NT):
                            last = dve.max(g8[:, t], gs[:, t])
                        link(last)
                        link(dve.memset(g8[:, :, TOP_GROUPS:], 3.0e38))
                        for t in range(NT):
                            last = dve.match_replace(gr[:, t], g8[:, t], gs[:, t], GONE)
                        link(last)
                        link(tt(gm[:], gr[:], gs[:], ALU.is_equal))
                        link(ts(gm[:], gm[:], GONE, None, ALU.mult))
                        link(tt(sel[:].rearrange("p t (g e) -> p t g e", g=GROUPS), sel[:].rearrange("p t (g e) -> p t g e", g=GROUPS),
                                gm[:].unsqueeze(3).to_broadcast([P, NT, GROUPS, per]), ALU.add))
                        for t in range(NT):
                            last = dve.max(g8[:, t], sel[:, t])
                        link(last)
                        for t in range(NT):
                            last = dve.match_replace(rep[:, t], g8[:, t], sel[:, t], 3.0e38)
                        link(last)
                        link(tt(m[:], rep[:], sel[:], ALU.not_equal))
                        link(dve.tensor_copy(mb[:], m[:]))
                        for t in range(NT):
                            ins = tt(cb[:, t + 1], cb[:, t], mb[:, t], ALU.add)
                            if t < NT - 1:
                                link(ins)
                        ins.then_inc(mask_done, 1)
                        link(tt(wt[:], sc[:], m[:], ALU.mult))
                        link(dve.tensor_reduce(tot[:], wt[:], AX, ALU.add))
                        link(dve.reciprocal(tot[:], tot[:]))
                        link(ts(tot[:], tot[:], SCALED, None, ALU.mult))
                        link(tt(wt[:], wt[:], tot[:].unsqueeze(2).to_broadcast([P, NT, E]), ALU.mult))
                        dve.wait_ge(iota_done, 1)
                        link(dve.tensor_copy(moving[:, :, :, 3], wt[:]))
                        link(tt(rest[:], wt[:], moving[:, :, :, 3], ALU.subtract))
                        link(dve.tensor_copy(moving[:, :, :, 4], rest[:]))
                        link(tt(rest[:], rest[:], moving[:, :, :, 4], ALU.subtract))
                        link(dve.tensor_copy(moving[:, :, :, 5], rest[:]))
                        dve.wait_ge(mm_done, 1)
                        pf = place[:].rearrange("p t e -> p (t e)")
                        link(dve.scalar_tensor_tensor(out=pf, in0=psP[:], scalar=1.0, in1=m[:].rearrange("p t e -> p (t e)"),
                                                      op0=ALU.add, op1=ALU.mult))
                        link(ts(pf, pf, -1.0, None, ALU.add))
                        link(dve.tensor_copy(cnt[:], psC[:]))
                        link(tt(cmp8[:], cnt[:].unsqueeze(2).to_broadcast([P, E, 8]),
                                ks[:].unsqueeze(1).to_broadcast([P, E, 8]), ALU.is_gt))
                        link(dve.tensor_reduce(nblk[:], cmp8[:], AX, ALU.add))
                        link(dve.memset(le[:], 0.0))
                        link(dve.tensor_tensor_scan(pend[:], nblk[:], le[:], 0.0, ALU.add, ALU.add))
                        for a in range(2):
                            b = small[:, 2 + a:3 + a]
                            link(ts(le[:], pend[:], b, None, ALU.is_le))
                            link(tt(lep[:], le[:], pend[:], ALU.mult))
                            link(dve.tensor_reduce(eb[:, a:a + 1], le[:], AX, ALU.add))
                            link(dve.tensor_reduce(kb[:, a:a + 1], lep[:], AX, ALU.max))
                        link(tt(kb[:], small[:, 2:4], kb[:], ALU.subtract))
                        link(ts(fb[:], eb[:], float(E), 8.0, ALU.is_ge, ALU.mult))
                        link(tt(kb[:], kb[:], fb[:], ALU.max))
                        link(ts(rowf[:, :, 1], kb[:], 8.0, None, ALU.min))
                        link(ts(rowf[:, :, 0], eb[:], float(E - 1), None, ALU.min))
                        link(ts(rowf[:, :, 2], rowf[:, :, 0], 1.0, None, ALU.add))
                        link(dve.tensor_copy(rowf[:, :, 3], rowf[:, :, 0]))
                        link(dve.tensor_copy(rowi[:], rowf[:]))
                        ts(rowi[:, :, 3], rowi[:, :, 3], RING - 1, None, ALU.bitwise_and).then_inc(rows_done, 1)
                        link(dve.tensor_copy(pends[0:1, 0:E], pend[0:1, :]))
                        link(ts(pends[0:1, E:E + 1], pend[0:1, E - 1:E], 0.5, -0.25, ALU.mult, ALU.add))

        def experts(layer, place, moving, table, pends, w_all):
            gathered, added = gather_sems[layer], scatter_sems[layer]
            E = EXPERTS
            with ExitStack() as ctx:
                sb, ps, sem = pools(ctx)
                ring = sb("ring", [P, RING, 3, KT * FF])
                slots = sb("slots", [P, 9 * P])
                small = sb("e_small", [P, 16])
                hot = sb("hot", [P, 2, NT, P], BF16)
                pick = sb("pick", [P, 6])
                pad = sb("pad", [P, 2])
                idx = sb("idx", [P, 2], U32)
                idx_all = sb("idx_all", [P, TABLE], U32)
                idx_out = sb("idx_out", [P, 2], U32)
                xg = sb("xg", [P, 2, D])
                xT = sb("xT", [P, 2, KT, P])
                e = sb("ex_e", [P, FF])
                hid = sb("ex_h", [P, 2, FF])
                hT = sb("ex_hT", [P, FF])
                yo = sb("ex_y", [P, 2, D])
                psG = [ps(f"exG{i}", [P, 2, FF]) for i in range(2)]
                psX = ps("exX", [P, KT, P])
                psD = ps("exD", [P, 2, 512])
                psI, psH = ps("exI", [P, 512]), ps("exH", [P, 512])
                w_in = [sem(f"w_in{i}") for i in range(RING)]
                c_in, landed = sem("ex_in"), sem("landed")
                hot_done, idx_mm, idx_done, X_mm = sem("hot_done"), sem("idx_mm"), sem("idx_done"), sem("X_mm")
                xT_a, xT_d, g_mm, e_done, h_done = (sem(n) for n in ("xT_a", "xT_d", "ex_g_mm", "ex_e_done", "ex_h_done"))
                H_mm, hT_done, d_mm, y_done, out_idx = (sem(n) for n in ("H_mm", "ex_hT_done", "ex_d_mm", "ex_y_done", "out_idx"))
                idx_own, h_own, all_added = sem("idx_own"), sem("ex_h_own"), sem("all_added")
                wg = A["exp_w_gate"][layer].rearrange("e (p k) n -> e p (k n)", k=KT)
                wu = A["exp_w_up"][layer].rearrange("e (p k) n -> e p (k n)", k=KT)
                wd = A["exp_w_down"][layer].rearrange("e (p k) n -> e p (k n)", k=FK)

                def turns(eng):
                    return eng.value_load(pends[0:1, E:E + 1], min_val=4, max_val=63)

                def loop(eng, body):
                    n = turns(eng)
                    body(1, 1, 0)
                    body(2, 0, 0)
                    with eng.Fori(1, n) as i:
                        body(2 * i + 1, 1, i)
                        body(2 * i + 2, 0, i)
                    return n

                def row(eng, b, c, hi):
                    return eng.value_load(table[0:1, ds(b * 4 + c, 1)], min_val=0, max_val=hi)

                with nc.Block() as block:
                    @block.sync
                    def _(sp):
                        sp.dma_start(slots[:], A["slots"]).then_inc(c_in, 16)
                        sp.dma_start(small[:], A["small"]).then_inc(c_in, 16)

                        def load(ex, r):
                            for j, src in enumerate((wg, wu, wd)):
                                sp.dma_start(ring[:, r, j], src[ds(ex, 1)].rearrange("a p n -> (a p) n")).then_inc(w_in[r], 16)

                        def land(r, turn):
                            sp.wait_ge(w_in[r], turn * 48 + 48)
                            sp.sem_inc(landed, 1)
                        for r in range(RING):
                            load(r, r)
                            if r >= 2:
                                land(r - 2, 0)
                        with sp.Fori(1, E // RING) as i:
                            for r in range(RING):
                                land((r + 2) % RING, i - 1 if r < 2 else i)
                                used = sp.value_load(pends[0:1, ds(i * RING + r - RING, 1)], min_val=0, max_val=127)
                                sp.wait_ge(d_mm, used + 1)
                                settle(sp, waited)
                                load(i * RING + r, r)
                        for r in range(2, RING):
                            land(r, E // RING - 1)

                    @block.gpsimd
                    def _(pool):
                        def gather(b, par):
                            pool.wait_ge(idx_done, b + 1)
                            after(pool, X_mm, b, 2)
                            settle(pool, waited)
                            pool.indirect_dma_start(out=xg[:, par], out_offset=None, in_=u_dram,
                                                    in_offset=bass.IndirectOffsetOnAxis(ap=idx[:, par:par + 1], axis=0)
                                                    ).then_inc(gathered[par], 16)

                        def add(b, par, before):
                            pool.wait_ge(y_done, b + 1)
                            pool.wait_ge(out_idx, b + 1)
                            at_least(pool, added[1 - par], before)
                            settle(pool, waited)
                            pool.indirect_dma_start(out=y_dram, out_offset=bass.IndirectOffsetOnAxis(ap=idx_out[:, par:par + 1], axis=0),
                                                    in_=yo[:, par], in_offset=None, compute_op=ALU.add).then_inc(added[par], 16)
                        for b in range(4):
                            gather(b, b % 2)

                        def body(b, par, i):
                            gather(b + 3, 1 - par)
                            add(b - 1, 1 - par, i * 16 if par else i * 16 + 16)
                        n = loop(pool, body)
                        add(n * 2, 0, n * 16)
                        pool.wait_ge(added[0], n * 16 + 16)
                        pool.sem_inc(all_added, 1)
                        pool.wait_ge(gathered[0], n * 16 + 32)
                        pool.sem_inc(all_added, 1)
                        pool.wait_ge(gathered[1], n * 16 + 32)
                        pool.sem_inc(all_added, 1)

                    @block.vector
                    def _(dve):
                        dve.wait_ge(c_in, 32)

                        def onehot(b, par):
                            ex, k = row(dve, b, 0, E - 1), row(dve, b, 1, 8)
                            after(dve, idx_mm, b, 2)
                            dve.tensor_tensor(hot[:, par], place[:, :, ds(ex, 1)].to_broadcast([P, NT, P]),
                                              slots[:, ds(k * P, P)].unsqueeze(1).to_broadcast([P, NT, P]),
                                              ALU.is_equal).then_inc(hot_done, 1)

                        def indices(b, par):
                            link = Links(dve, idx_own, b * 4)
                            dve.wait_ge(idx_mm, b + 1)
                            if not isinstance(b, int) or b >= 2:
                                dve.wait_ge(X_mm, b - 1)
                            link(dve.tensor_copy(pick[:], psI[:, 0:6]))
                            dve.tensor_reduce(w_all[:, ds(b, 1)], pick[:, 3:6], AX, ALU.add)
                            dve.tensor_reduce(pad[:, 0:1], pick[:, 0:2], AX, ALU.add)
                            link(dve.tensor_scalar(pad[:, 1:2], pick[:, 2:3], small[:, 1:2], small[:, 0:1], ALU.mult, ALU.add))
                            link(dve.tensor_tensor(idx_all[:, ds(b, 1)], pad[:, 0:1], pad[:, 1:2], ALU.add))
                            link(dve.tensor_tensor(idx[:, par:par + 1], pad[:, 0:1], pad[:, 1:2], ALU.add))
                            assert link.n == 4
                            dve.sem_inc(idx_done, 1)

                        def rows(b, par):
                            dve.wait_ge(X_mm, b + 1)
                            after(dve, g_mm, b, 2)
                            dve.tensor_copy(xT[:, par, 0:KT // 2], psX[:, 0:KT // 2]).then_inc(xT_d, 1)

                        def hidden(b, par):
                            link = Links(dve, h_own, b * 3)
                            dve.wait_ge(e_done, b + 1)
                            link(dve.tensor_scalar(e[:], e[:], 1.0, None, ALU.add))
                            link(dve.reciprocal(e[:], e[:]))
                            link(dve.tensor_tensor(e[:], psG[par][:, 0], e[:], ALU.mult))
                            after(dve, H_mm, b, 2)
                            dve.tensor_tensor(hid[:, par].rearrange("t (k p) -> t p k", k=FK),
                                              e[:].rearrange("t (p k) -> t p k", k=FK),
                                              psG[par][:, 1].rearrange("t (p k) -> t p k", k=FK), ALU.mult).then_inc(h_done, 1)

                        def targets(b, par):
                            if not isinstance(b, int) or b >= 2:
                                dve.wait_ge(added[par], (b - par) * 8)
                            dve.tensor_copy(idx_out[:, par:par + 1], idx_all[:, ds(b, 1)]).then_inc(out_idx, 1)

                        onehot(0, 0)
                        onehot(1, 1)
                        indices(0, 0)
                        onehot(2, 0)
                        indices(1, 1)
                        rows(0, 0)
                        indices(2, 0)
                        onehot(3, 1)
                        rows(1, 1)
                        indices(3, 1)
                        hidden(0, 0)

                        def body(b, par, i):
                            onehot(b + 3, 1 - par)
                            rows(b + 1, 1 - par)
                            indices(b + 3, 1 - par)
                            hidden(b, par)
                            targets(b - 1, 1 - par)
                        n = loop(dve, body)
                        targets(n * 2, 0)

                    @block.scalar
                    def _(act):
                        def rows(b, par):
                            act.wait_ge(X_mm, b + 1)
                            after(act, g_mm, b, 2)
                            act.activation(xT[:, par, KT // 2:], psX[:, KT // 2:], ACT.Copy).then_inc(xT_a, 1)

                        def gates(b, par):
                            act.wait_ge(g_mm, b + 1)
                            after(act, h_done, b, 1)
                            act.activation(e[:], psG[par][:, 0], ACT.Exp, scale=-1.0).then_inc(e_done, 1)

                        def turned(b):
                            act.wait_ge(H_mm, b + 1)
                            at_least(act, d_mm, b + 1)
                            act.activation(hT[:], psH[:, 0:FF], ACT.Copy).then_inc(hT_done, 1)

                        def weigh(b, par):
                            act.wait_ge(d_mm, b + 2)
                            if not isinstance(b, int) or b >= 2:
                                act.wait_ge(added[par], (b - par) * 8)
                            act.activation(yo[:, par], psD[:].rearrange("p a b -> p (a b)"), ACT.Copy,
                                           scale=w_all[:, ds(b, 1)]).then_inc(y_done, 1)
                        rows(0, 0)
                        rows(1, 1)
                        gates(0, 0)

                        def body(b, par, i):
                            turned(b - 1)
                            rows(b + 1, 1 - par)
                            gates(b, par)
                            weigh(b - 1, 1 - par)
                        n = loop(act, body)
                        turned(n * 2)
                        weigh(n * 2, 0)

                    @block.tensor
                    def _(pe):
                        def index(b, par):
                            ex = row(pe, b, 0, E - 1)
                            pe.wait_ge(hot_done, b + 1)
                            if not isinstance(b, int) or b >= 1:
                                pe.wait_ge(idx_own, b * 4 - 3)
                            for t in range(NT):
                                last = pe.matmul(psI[:, 0:6], hot[:, par, t], moving[:, t, ds(ex, 1), :].rearrange("p a c -> p (a c)"),
                                                 start=t == 0, stop=t == NT - 1)
                            last.then_inc(idx_mm, 1)

                        def turn_rows(b, par, landed_at):
                            pe.wait_ge(gathered[par], landed_at)
                            if not isinstance(b, int) or b >= 1:
                                pe.wait_ge(xT_a, b)
                                pe.wait_ge(xT_d, b)
                            for k in range(KT):
                                last = pe.transpose(psX[:, k], xg[:, par, k * P:(k + 1) * P], ident[:])
                            last.then_inc(X_mm, 1)

                        def gate_up(b, par):
                            weights, slot = row(pe, b, 2, E), row(pe, b, 3, RING - 1)
                            pe.wait_ge(landed, weights)
                            pe.wait_ge(xT_a, b + 1)
                            pe.wait_ge(xT_d, b + 1)
                            after(pe, h_done, b, 2)
                            for k in range(KT):
                                last = pe.matmul(psG[par][:], xT[:, par, k],
                                                 ring[:, ds(slot, 1), 0:2, k * FF:(k + 1) * FF].rearrange("p a j n -> p (a j) n"),
                                                 start=k == 0, stop=k == KT - 1)
                            last.then_inc(g_mm, 1)

                        def turn_hidden(b, par):
                            pe.wait_ge(h_done, b + 1)
                            after(pe, hT_done, b, 1)
                            for k in range(FK):
                                last = pe.transpose(psH[:, k * P:(k + 1) * P], hid[:, par, k * P:(k + 1) * P], ident[:])
                            last.then_inc(H_mm, 1)

                        def down(b):
                            slot = row(pe, b, 3, RING - 1)
                            pe.wait_ge(hT_done, b + 1)
                            after(pe, y_done, b, 1)
                            for c in range(2):
                                for k in range(FK):
                                    last = pe.matmul(psD[:, c], hT[:, k * P:(k + 1) * P],
                                                     ring[:, ds(slot, 1), 2, k * D + c * 512:k * D + (c + 1) * 512].rearrange("p a n -> p (a n)"),
                                                     start=k == 0, stop=k == FK - 1)
                            last.then_inc(d_mm, 1)

                        pe.sem_inc(d_mm, 1)
                        index(0, 0)
                        index(1, 1)
                        turn_rows(0, 0, 16)
                        index(2, 0)
                        gate_up(0, 0)
                        turn_rows(1, 1, 16)
                        index(3, 1)

                        def body(b, par, i):
                            gate_up(b, par)
                            turn_hidden(b - 1, 1 - par)
                            turn_rows(b + 1, 1 - par, i * 16 + 32)
                            index(b + 3, 1 - par)
                            down(b - 1)
                        n = loop(pe, body)
                        turn_hidden(n * 2, 0)
                        down(n * 2)

        def finish(layer, last):
            with ExitStack() as ctx:
                sb, ps, sem = pools(ctx)
                y = sb("y_in", [P, 2, D])
                z = sb("fz", [P, D])
                xo = sb("fx", [P, 2, D])
                lnp = sb("lnp2", [P, 2, D])
                ln_in = sem("ln_in")
                r = root(ctx, sem)
                y_in, x_out = [sem(f"y_in{i}") for i in range(2)], [sem(f"x_out{i}") for i in range(2)]
                own, x_done = sem("fin_own"), sem("x_done")
                dst = (out[0].rearrange("(p t) d -> t p d", t=NT) if last else x_dram.rearrange("(t p) d -> t p d", p=P))
                with nc.Block() as block:
                    @block.sync
                    def _(sp):
                        def load(t, par):
                            sp.dma_start(y[:, par], y_dram[ds(t * P, P), :]).then_inc(y_in[par], 16)

                        def store(t, par):
                            sp.wait_ge(x_done, t + 1)
                            sp.dma_start(dst[ds(t, 1)].rearrange("a p d -> (a p) d"), xo[:, par]).then_inc(x_out[par], 16)
                        for j, name in enumerate(("ln_g", "ln_b")):
                            sp.dma_start(lnp[:, j], A[name][layer, 1:2].to_broadcast([P, D])).then_inc(ln_in, 16)
                        load(0, 0)
                        load(1, 1)
                        with sp.Fori(0, NT // 2 - 1) as i:
                            for par in range(2):
                                store(2 * i + par, par)
                                load(2 * i + par + 2, par)
                        for par in range(2):
                            store(NT - 2 + par, par)
                        for par in range(2):
                            sp.wait_ge(x_out[par], 16 * (NT // 2))

                    @block.gpsimd
                    def _(pool):
                        roots(pool, r, NT)

                    @block.vector
                    def _(dve):
                        def body(t, par):
                            link = Links(dve, own, t * 6)
                            after(dve, x_done, t, 1)
                            dve.wait_ge(y_in[par], (t - par) * 8 + 16)
                            if not isinstance(t, int) or t >= 2:
                                dve.wait_ge(x_out[par], (t - par) * 8)
                            post_norm(dve, link, r, y[:, par], z[:], tile(x, t), xo[:, par], gate2, lnp, t + 1).then_inc(x_done, 1)
                            assert link.n == 6
                        dve.wait_ge(ln_in, 32)
                        steps(dve, NT, 2, 0, body)

        def fourier(fT):
            with ExitStack() as ctx:
                sb, ps, sem = pools(ctx)
                u = sb("f_u", [P, NT, D])
                feat = sb("feat", [P, FGW // P, 2 * FGW])
                tok = sb("tok", [P, NT, 2, P])
                Z = sb("Z", [P, NT, FGW])
                T = sb("Ztmp", [P, NT, FGW])
                ZT = sb("ZT", [P, NT, FGW // P, P])
                C = sb("f_c", [P, 2, 2 * FGW])
                G = sb("f_g", [P, NT, 2, FGW])
                r = root(ctx, sem)
                psZ = ps("fZ", [P, 2, 512])
                psF = ps("fF", [P, 2, 512])
                psO = ps("fO", [P, 2, 512])
                w_in, own, fown = sem("f_in"), sem("f_own"), sem("f_fown")
                x_in, u_done = sem("x_in"), sem("f_u_done")
                Z_done, ZT_mm, ZT_done, F_mm, C_done, G_done, C_used = (sem(n) for n in (
                    "Z_done", "ZT_mm", "ZT_done", "F_mm", "C_done", "G_done", "C_used"))
                O_mm, O_done = sem("O_mm"), sem("O_done")
                KG = FGW // P
                NA = NT
                with nc.Block() as block:
                    @block.sync
                    def _(sp):
                        sp.dma_start(x[:], x_dram.rearrange("(t p) d -> p t d", p=P)).then_inc(x_in, 16)
                        sp.dma_start(feat[:].rearrange("p a b -> p (a b)"), A["feat"]).then_inc(w_in, 16)
                        sp.dma_start(tok[:].rearrange("p a b c -> p (a b c)"), A["tok"]).then_inc(w_in, 16)
                        sp.wait_ge(u_done, NT)
                        sp.dma_start(x[:], x_dram.rearrange("(p t) d -> p t d", t=NT)).then_inc(x_in, 16)
                        sp.wait_ge(x_in, 32)

                    @block.gpsimd
                    def _(pool):
                        roots(pool, r, NT)

                    @block.vector
                    def _(dve):
                        dve.wait_ge(x_in, 16)
                        with dve.Fori(0, NT) as t:
                            link = Links(dve, own, t * 5)
                            normalise(dve, link, r, tile(x, t), tile(u, t), MOD_EPS, t + 1)
                            link(dve.tensor_tensor(tile(u, t), tile(u, t), scale1, ALU.mult))
                            link(dve.tensor_tensor(tile(u, t), tile(u, t), shift1, ALU.add))
                            dve.sem_inc(u_done, 1)
                        dve.wait_ge(w_in, 32)
                        K1 = 3
                        def group(g):
                            link = Links(dve, fown, g * K1)
                            tt = dve.tensor_tensor
                            c = ds(g * FGW, FGW)
                            half = NT // 2
                            at_least(dve, Z_done, g)
                            tt(T[:, 0:half], u[:, 0:half, c], u[:, half:, c], ALU.add)
                            link(tt(T[:, half:], u[:, 0:half, c], u[:, half:, c], ALU.subtract))
                            at_least(dve, ZT_mm, g * NA)
                            tt(Z[:, 4], T[:, 0], T[:, 2], ALU.subtract)
                            tt(Z[:, 5], T[:, 3], T[:, 1], ALU.subtract)
                            tt(Z[:, 0], T[:, 0], T[:, 2], ALU.add)
                            tt(Z[:, 1], T[:, 1], T[:, 3], ALU.add)
                            tt(Z[:, 2], T[:, 5], T[:, 7], ALU.subtract)
                            link(tt(Z[:, 3], T[:, 5], T[:, 7], ALU.add))
                            R = float(np.sqrt(0.5))
                            tt(T[:, 0], Z[:, 0], Z[:, 1], ALU.add)
                            tt(T[:, 1], Z[:, 0], Z[:, 1], ALU.subtract)
                            stt = dve.scalar_tensor_tensor
                            stt(out=Z[:, 6], in0=Z[:, 2], scalar=-R, in1=T[:, 4], op0=ALU.mult, op1=ALU.add)
                            stt(out=Z[:, 7], in0=Z[:, 3], scalar=-R, in1=T[:, 6], op0=ALU.mult, op1=ALU.add)
                            stt(out=T[:, 2], in0=Z[:, 2], scalar=R, in1=T[:, 4], op0=ALU.mult, op1=ALU.add)
                            link(stt(out=T[:, 3], in0=Z[:, 3], scalar=-R, in1=T[:, 6], op0=ALU.mult, op1=ALU.subtract))
                            dve.tensor_copy(Z[:, 0], T[:, 0])
                            dve.tensor_copy(Z[:, 1], T[:, 1])
                            dve.tensor_copy(Z[:, 2], T[:, 2])
                            dve.tensor_copy(Z[:, 3], T[:, 3]).then_inc(Z_done, 1)
                            for j, k1 in enumerate((1, 2, 3)):
                                a = g * 5 + 2 + j
                                dve.wait_ge(C_done, a + 1)
                                dve.wait_ge(F_mm, g * NA + 4 + 2 * j)
                                re_, im = C[:, k1 % 2], psF[:, 1]
                                at_least(dve, O_mm, g * KG)
                                tt(G[:, k1, 0], re_[:, 0:FGW], im[:, FGW:], ALU.add)
                                tt(G[:, NT - k1, 0], re_[:, 0:FGW], im[:, FGW:], ALU.subtract)
                                tt(G[:, k1, 1], im[:, 0:FGW], re_[:, FGW:], ALU.subtract)
                                stt(out=G[:, NT - k1, 1], in0=im[:, 0:FGW], scalar=-1.0, in1=re_[:, FGW:],
                                    op0=ALU.mult, op1=ALU.subtract).then_inc(C_used, 1)
                            assert link.n == 3
                        rounds(dve, FG, group)

                    @block.scalar
                    def _(act):
                        def group(g):
                            for a in range(NA // 2):
                                act.wait_ge(ZT_mm, g * NA + 2 * a + 2)
                                act.activation(ZT[:, 2 * a:2 * a + 2].rearrange("p a k c -> p (a k c)"), psZ[:, a % 2], ACT.Copy).then_inc(ZT_done, 1)
                            at_least(act, O_mm, g * KG)
                            for j, k1 in enumerate((0, NT // 2)):
                                act.wait_ge(F_mm, g * NA + j + 1)
                                act.activation(G[:, k1, 0], psF[:, j % 2, 0:FGW], ACT.Copy)
                                act.activation(G[:, k1, 1], psF[:, j % 2, FGW:], ACT.Copy, scale=-1.0).then_inc(C_done, 1)
                            for j, k1 in enumerate((1, 2, 3)):
                                act.wait_ge(F_mm, g * NA + 3 + 2 * j)
                                at_least(act, C_used, g * 3 + max(j - 1, 0))
                                act.activation(C[:, k1 % 2], psF[:, 0], ACT.Copy).then_inc(C_done, 1)
                            for k in range(KG):
                                act.wait_ge(O_mm, g * KG + k + 1)
                                act.activation(fT[:, ds(g * KG + k, 1), :].rearrange("p a c -> p (a c)"),
                                               psO[:].rearrange("p a b -> p (a b)"), ACT.Copy).then_inc(O_done, 1)
                        rounds(act, FG, group)

                    @block.tensor
                    def _(pe):
                        pe.wait_ge(w_in, 32)
                        def group(g):
                            pe.wait_ge(Z_done, g + 1)
                            for a in range(NA):
                                if a % 2 == 0:
                                    at_least(pe, ZT_done, g * (NA // 2) + max(a // 2 - 1, 0))
                                for k in range(KG):
                                    last = pe.transpose(psZ[:, a // 2 % 2, (a % 2 * KG + k) * P:(a % 2 * KG + k + 1) * P],
                                                        Z[:, a, k * P:(k + 1) * P], ident[:])
                                last.then_inc(ZT_mm, 1)
                            for a in range(NA):
                                if a % 2 == 0:
                                    pe.wait_ge(ZT_done, g * (NA // 2) + a // 2 + 1)
                                if a < 2:
                                    at_least(pe, C_used, g * 3)
                                elif a < 4:
                                    pe.wait_ge(C_done, g * 5 + a - 1)
                                elif a % 2 == 0:
                                    pe.wait_ge(C_done, g * 5 + 2 + a // 2 - 1)
                                else:
                                    pe.wait_ge(C_used, g * 3 + a // 2 - 1)
                                for k in range(KG):
                                    last = pe.matmul(psF[:, a % 2], ZT[:, a, k], feat[:, k], start=k == 0, stop=k == KG - 1)
                                last.then_inc(F_mm, 1)
                            pe.wait_ge(C_used, g * 3 + 3)
                            for k in range(KG):
                                at_least(pe, O_done, g * KG + k)
                                for k1 in range(NT):
                                    o = psO[:, k1 // 4, (k1 % 4) * P:(k1 % 4 + 1) * P]
                                    pe.matmul(o, G[:, k1, 0, k * P:(k + 1) * P], tok[:, k1, 0], start=True, stop=False)
                                    last = pe.matmul(o, G[:, k1, 1, k * P:(k + 1) * P], tok[:, k1, 1], start=False, stop=True)
                                last.then_inc(O_mm, 1)
                        rounds(pe, FG, group)

        def show(t_src, tiled=False):
            with ExitStack() as ctx:
                _, _, sem = pools(ctx)
                s_out = sem("s_out")
                with nc.Block() as block:
                    @block.sync
                    def _(sp):
                        sp.dma_start(out[0].rearrange("(t p) d -> p t d", p=P) if tiled else out[0], t_src).then_inc(s_out, 16)
                        sp.wait_ge(s_out, 16)

        def moe(layer, logits):
            with ExitStack() as ctx:
                sb, _, _ = pools(ctx)
                place = sb("place", [P, NT, EXPERTS])
                moving = sb("moving", [P, NT, EXPERTS, 6], BF16)
                table = sb("table", [1, TABLE * 4], I32)
                pends = sb("pends", [1, EXPERTS + 1], I32)
                w_all = sb("w_all", [P, TABLE])
                route(layer, logits, place, moving, table, pends, w_all)
                experts(layer, place, moving, table, pends, w_all)

        logits = whole.enter_context(nc.sbuf_tensor("logits", [P, NT, EXPERTS], F32))
        with ExitStack() as ctx:
            sb, _, _ = pools(ctx)
            kT = sb("kT", [P, KV_HEADS, KSLOTS * P])
            v = sb("v", [P, KSLOTS, KVW])
            with ExitStack() as inner:
                modc = inner.enter_context(nc.sbuf_tensor("modc", [P, 2 * D], F32))
                ada(0, modc)
                project_qkv(kT, v, modc)
            attend(kT, v)
        if stop == "att":
            return show(o_dram)
        mix(0, o_dram, False, A["attn_w_o"][0], logits)
        if stop == "mix":
            return show(x[:], True)
        moe(0, logits)
        finish(0, False)
        if stop == "l0":
            return show(x_dram)
        ada(1)
        with ExitStack() as ctx:
            sb, _, _ = pools(ctx)
            fT = sb("fT", [P, KT, SEQ])
            fourier(fT)
            mix(1, fT, True, A["fnet_w"][0], logits)
        moe(1, logits)
        finish(1, True)


_INS = ["x", "c", "ctx", "c_ctx", "w_ada", "b_ada", "ln_g", "ln_b", "attn_w_qkv", "attn_w_o", "attn_sinks", "fnet_w",
        "router_w", "router_bias", "exp_w_gate", "exp_w_up", "exp_w_down", "sh_w_gate", "sh_w_up", "sh_w_down"]
STOP = None


def kernel(**inputs):
    import concourse.bacc as _bacc
    from concourse.bass_utils import run_bass_kernel_spmd as _run

    nc = _bacc.Bacc("TRN2", target_bir_lowering=False, num_devices=1)
    arrays, args = {}, {}
    for name, a in [(n, inputs[n]) for n in _INS] + list(constants().items()):
        a = np.ascontiguousarray(a)
        arrays[f"in_{name}_dram"] = a
        args[name] = nc.dram_tensor(f"in_{name}_dram", a.shape, mybir.dt.from_np(a.dtype), kind="ExternalInput").ap()
    out = nc.dram_tensor("out_0_dram", (1, SEQ, D), F32, kind="ExternalOutput").ap()
    trunk(nc, args, out, STOP)
    r = _run(nc, [arrays], core_ids=[0])
    return r.results[0]["out_0_dram"]
```
